# Optimizing a Trainium2 kernel written in Bass

```python
import jax, jax.numpy as jnp
from jax import lax
import numpy as np

D_MODEL = 1024
BATCH = 1
SEQ = 1024
DEPTH = 1
DEC_BATCH = 8
DEC_SEQ = 16
PAST_LEN = 128

CHUNK = 64
Q_BLOCK = 128
HEAD_DIM = 64
SB_HEADS = 8
FOX_HEADS = 8
SB_WIDTH = SB_HEADS * HEAD_DIM
FOX_WIDTH = FOX_HEADS * HEAD_DIM
IN_WIDTH = 3 * SB_WIDTH + 3 * FOX_WIDTH + FOX_HEADS
N_GROUPS = 4
EXPERTS_PER_GROUP = 4
N_EXPERTS = N_GROUPS * EXPERTS_PER_GROUP
TOP_K = 2
EXPERT_HIDDEN = 256
N_MOD = 6
RMS_EPS = 1e-6

kernel_name = 'stickbreak_fox_hmoe_stream_step'

def rmsnorm(x, g):
    xf = x.astype(jnp.float32)
    y = xf * lax.rsqrt(jnp.mean(xf * xf, axis=-1, keepdims=True) + RMS_EPS)
    return (y * g.astype(jnp.float32)).astype(x.dtype)

def to_heads(a, n_heads):
    b, t, _ = a.shape
    return a.reshape(b, t, n_heads, HEAD_DIM).transpose(0, 2, 1, 3)

def from_heads(a):
    b, h, t, d = a.shape
    return a.transpose(0, 2, 1, 3).reshape(b, t, h * d)

def sb_attend(q_pos, q, k, v, k_pos):
    z = jnp.einsum('bhqd,bhkd->bhqk', q.astype(jnp.float32), k.astype(jnp.float32)) * (HEAD_DIM ** -0.5)
    mask = k_pos[None, :] < q_pos[:, None]
    log_skip = jnp.where(mask, jax.nn.log_sigmoid(-z), 0.0)
    later = lax.cumsum(log_skip, axis=3, reverse=True) - log_skip
    w = jnp.where(mask, jnp.exp(jax.nn.log_sigmoid(z) + later), 0.0)
    return jnp.einsum('bhqk,bhkd->bhqd', w, v.astype(jnp.float32)).astype(v.dtype)

def fox_attend(q_pos, q, fq, k, v, k_pos, fk):
    z = jnp.einsum('bhqd,bhkd->bhqk', q.astype(jnp.float32), k.astype(jnp.float32)) * (HEAD_DIM ** -0.5)
    z = z + fq[..., :, None] - fk[..., None, :]
    z = jnp.where(k_pos[None, :] <= q_pos[:, None], z, -jnp.inf)
    p = jax.nn.softmax(z, axis=-1)
    return jnp.einsum('bhqk,bhkd->bhqd', p, v.astype(jnp.float32)).astype(v.dtype)

def sweep_queries(attend, q_pos, *q_side):
    t = q_pos.shape[0]
    if t % Q_BLOCK != 0 or t <= Q_BLOCK:
        return attend(q_pos, *q_side)
    nb = t // Q_BLOCK

    def split(a):
        a = a.reshape(a.shape[:2] + (nb, Q_BLOCK) + a.shape[3:])
        return jnp.moveaxis(a, 2, 0)

    out = lax.map(lambda blk: attend(blk[0], *blk[1]),
                  (q_pos.reshape(nb, Q_BLOCK), tuple(split(a) for a in q_side)))
    out = jnp.moveaxis(out, 0, 2)
    return out.reshape(out.shape[:2] + (t,) + out.shape[4:])

def hier_moe(h, w_rg, b_rg, w_re, b_re, w1, w3, w2):
    b, t, d = h.shape
    tok = h.reshape(b * t, d)
    g_prob = jax.nn.softmax((tok @ w_rg + b_rg).astype(jnp.float32), axis=-1)
    g_idx = jnp.argmax(g_prob, axis=-1)
    g_w = jnp.take_along_axis(g_prob, g_idx[:, None], axis=1)
    e_logits = (tok @ w_re + b_re).astype(jnp.float32).reshape(-1, N_GROUPS, EXPERTS_PER_GROUP)
    e_sel = jnp.take_along_axis(e_logits, g_idx[:, None, None], axis=1)[:, 0]
    e_prob = jax.nn.softmax(e_sel, axis=-1)
    top_w, top_i = lax.top_k(e_prob, TOP_K)
    top_w = top_w / jnp.sum(top_w, axis=-1, keepdims=True)
    expert_id = g_idx[:, None] * EXPERTS_PER_GROUP + top_i
    combine = jnp.sum(jax.nn.one_hot(expert_id, N_EXPERTS, dtype=jnp.float32)
                      * (g_w * top_w)[..., None], axis=1).astype(h.dtype)
    out = jnp.zeros_like(tok)
    for e in range(N_EXPERTS):
        act = jax.nn.silu(tok @ w1[e]) * (tok @ w3[e])
        out = out + combine[:, e:e + 1] * (act @ w2[e])
    return out.reshape(b, t, d)

def trunk_layer(x, c, past_sb_k, past_sb_v, past_fox_k, past_fox_v, past_fox_logf,
                w_ada, b_ada, g_mix, w_in, b_f, w_ba, w_bb, w_gate, b_gate, w_out,
                g_moe, w_rg, b_rg, w_re, b_re, w1, w3, w2):
    t = x.shape[1]
    p_len = past_sb_k.shape[2]
    ada = (jax.nn.silu(c) @ w_ada + b_ada)[:, None, :]
    shift1, scale1, gate1, shift2, scale2, gate2 = jnp.split(ada, N_MOD, axis=-1)

    h = rmsnorm(x, g_mix) * (1.0 + scale1) + shift1
    proj = h @ w_in
    cuts = [SB_WIDTH, 2 * SB_WIDTH, 3 * SB_WIDTH, 3 * SB_WIDTH + FOX_WIDTH,
            3 * SB_WIDTH + 2 * FOX_WIDTH, 3 * SB_WIDTH + 3 * FOX_WIDTH]
    qa, ka, va, qb, kb, vb, fg = jnp.split(proj, cuts, axis=-1)
    qa, ka, va = to_heads(qa, SB_HEADS), to_heads(ka, SB_HEADS), to_heads(va, SB_HEADS)
    qb, kb, vb = to_heads(qb, FOX_HEADS), to_heads(kb, FOX_HEADS), to_heads(vb, FOX_HEADS)
    logf = jax.nn.log_sigmoid((fg + b_f).astype(jnp.float32)).transpose(0, 2, 1)

    q_pos = p_len + jnp.arange(t)
    k_pos = jnp.arange(p_len + t)
    k_sb = jnp.concatenate([past_sb_k.astype(ka.dtype), ka], axis=2)
    v_sb = jnp.concatenate([past_sb_v.astype(va.dtype), va], axis=2)
    k_fx = jnp.concatenate([past_fox_k.astype(kb.dtype), kb], axis=2)
    v_fx = jnp.concatenate([past_fox_v.astype(vb.dtype), vb], axis=2)
    f_all = jnp.cumsum(jnp.concatenate([past_fox_logf.astype(jnp.float32), logf], axis=2), axis=2)
    f_q = f_all[:, :, p_len:]

    ya = sweep_queries(lambda qp, qq: sb_attend(qp, qq, k_sb, v_sb, k_pos), q_pos, qa)
    yb = sweep_queries(lambda qp, qq, ff: fox_attend(qp, qq, ff, k_fx, v_fx, k_pos, f_all), q_pos, qb, f_q)
    ua = from_heads(ya) @ w_ba
    ub = from_heads(yb) @ w_bb
    ga, gb = jnp.split(jax.nn.sigmoid(h @ w_gate + b_gate), 2, axis=-1)
    x = x + gate1 * ((ga * ua + gb * ub) @ w_out)

    h2 = rmsnorm(x, g_moe) * (1.0 + scale2) + shift2
    x = x + gate2 * hier_moe(h2, w_rg, b_rg, w_re, b_re, w1, w3, w2)
    return x, ka, va, kb, vb, logf

def setup_inputs(seed: int = 0) -> dict:
    key = jax.random.key(seed)
    ks = jax.random.split(key, 32)
    f32 = jnp.float32

    def nrm(k, shape, scale):
        return jax.random.normal(k, shape, f32) * scale

    d = D_MODEL
    return {
        'x_prompt': nrm(ks[0], (BATCH, SEQ, d), 1.0),
        'x_sample': nrm(ks[1], (DEC_BATCH, DEC_SEQ, d), 1.0),
        'cache_sb_k': nrm(ks[2], (DEPTH, DEC_BATCH, SB_HEADS, PAST_LEN, HEAD_DIM), 1.0),
        'cache_sb_v': nrm(ks[3], (DEPTH, DEC_BATCH, SB_HEADS, PAST_LEN, HEAD_DIM), 1.0),
        'cache_fox_k': nrm(ks[4], (DEPTH, DEC_BATCH, FOX_HEADS, PAST_LEN, HEAD_DIM), 1.0),
        'cache_fox_v': nrm(ks[5], (DEPTH, DEC_BATCH, FOX_HEADS, PAST_LEN, HEAD_DIM), 1.0),
        'cache_fox_logf': jax.nn.log_sigmoid(2.0 + nrm(ks[6], (DEPTH, DEC_BATCH, FOX_HEADS, PAST_LEN), 1.0)),
        'c_prompt': nrm(ks[7], (BATCH, d), 1.0),
        'c_sample': nrm(ks[8], (DEC_BATCH, d), 1.0),
        'w_ada': nrm(ks[9], (DEPTH, d, N_MOD * d), d ** -0.5),
        'b_ada': nrm(ks[10], (DEPTH, N_MOD * d), 0.01),
        'g_mix': 1.0 + nrm(ks[11], (DEPTH, d), 0.02),
        'w_in': nrm(ks[12], (DEPTH, d, IN_WIDTH), d ** -0.5),
        'b_f': 2.0 + nrm(ks[13], (DEPTH, FOX_HEADS), 0.1),
        'w_ba': nrm(ks[14], (DEPTH, SB_WIDTH, d), SB_WIDTH ** -0.5),
        'w_bb': nrm(ks[15], (DEPTH, FOX_WIDTH, d), FOX_WIDTH ** -0.5),
        'w_gate': nrm(ks[16], (DEPTH, d, 2 * d), d ** -0.5),
        'b_gate': nrm(ks[17], (DEPTH, 2 * d), 0.01),
        'w_out': nrm(ks[18], (DEPTH, d, d), d ** -0.5),
        'g_moe': 1.0 + nrm(ks[19], (DEPTH, d), 0.02),
        'w_rg': nrm(ks[20], (DEPTH, d, N_GROUPS), d ** -0.5),
        'b_rg': nrm(ks[21], (DEPTH, N_GROUPS), 0.01),
        'w_re': nrm(ks[22], (DEPTH, d, N_EXPERTS), d ** -0.5),
        'b_re': nrm(ks[23], (DEPTH, N_EXPERTS), 0.01),
        'w1': nrm(ks[24], (DEPTH, N_EXPERTS, d, EXPERT_HIDDEN), d ** -0.5),
        'w3': nrm(ks[25], (DEPTH, N_EXPERTS, d, EXPERT_HIDDEN), d ** -0.5),
        'w2': nrm(ks[26], (DEPTH, N_EXPERTS, EXPERT_HIDDEN, d), EXPERT_HIDDEN ** -0.5),
        'g_final': 1.0 + nrm(ks[27], (d,), 0.02),
    }

def reference(x_prompt, x_sample, cache_sb_k, cache_sb_v, cache_fox_k, cache_fox_v, cache_fox_logf,
              c_prompt, c_sample, w_ada, b_ada, g_mix, w_in, b_f, w_ba, w_bb, w_gate, b_gate, w_out,
              g_moe, w_rg, b_rg, w_re, b_re, w1, w3, w2, g_final):
    xp, xs = x_prompt, x_sample
    psk, psv, pfk, pfv, pfl = [], [], [], [], []
    ssk, ssv, sfk, sfv, sfl = [], [], [], [], []
    for l in range(DEPTH):
        weights = (w_ada[l], b_ada[l], g_mix[l], w_in[l], b_f[l], w_ba[l], w_bb[l], w_gate[l], b_gate[l],
                   w_out[l], g_moe[l], w_rg[l], b_rg[l], w_re[l], b_re[l], w1[l], w3[l], w2[l])
        empty_sb = jnp.zeros((xp.shape[0], SB_HEADS, 0, HEAD_DIM), xp.dtype)
        empty_fx = jnp.zeros((xp.shape[0], FOX_HEADS, 0, HEAD_DIM), xp.dtype)
        empty_lf = jnp.zeros((xp.shape[0], FOX_HEADS, 0), jnp.float32)
        xp, ka, va, kb, vb, lf = trunk_layer(xp, c_prompt, empty_sb, empty_sb, empty_fx, empty_fx, empty_lf, *weights)
        psk.append(ka); psv.append(va); pfk.append(kb); pfv.append(vb); pfl.append(lf)
        xs, ka, va, kb, vb, lf = trunk_layer(xs, c_sample, cache_sb_k[l], cache_sb_v[l], cache_fox_k[l],
                                             cache_fox_v[l], cache_fox_logf[l], *weights)
        ssk.append(ka); ssv.append(va); sfk.append(kb); sfv.append(vb); sfl.append(lf)
    y_prompt = rmsnorm(xp, g_final)
    y_sample = rmsnorm(xs, g_final)
    return (y_prompt, y_sample,
            jnp.stack(psk), jnp.stack(psv), jnp.stack(pfk), jnp.stack(pfv), jnp.stack(pfl),
            jnp.stack(ssk), jnp.stack(ssv), jnp.stack(sfk), jnp.stack(sfv), jnp.stack(sfl))


_drawn_inputs = setup_inputs


def setup_inputs(seed=0):
    import zlib

    import numpy as np

    out = dict(_drawn_inputs(seed))
    spreads = {}
    factors = {'b_gate': 22.662,
     'b_rg': 55.438,
     'b_re': 60.634,
     'g_final': 30.141,
     'g_mix': 2.779,
     'cache_fox_logf': 2.843,
     'g_moe': 3.749}
    for name, (base, spread) in spreads.items():
        noise = np.random.default_rng([zlib.crc32(name.encode()), seed]).standard_normal(out[name].shape)
        drawn = base * np.exp(spread * noise) if base else spread * noise
        out[name] = __import__('jax').numpy.asarray(drawn.astype(out[name].dtype))
    for name, factor in factors.items():
        out[name] = (out[name] * factor).astype(out[name].dtype)
    return out
```

```python
import concourse.bass as bass
from concourse import mybir
from contextlib import ExitStack

F32 = mybir.dt.float32
F32R = mybir.dt.float32r
BF16 = mybir.dt.bfloat16
I32 = mybir.dt.int32
ACT = mybir.ActivationFunctionType
ALU = mybir.AluOpType
AX = mybir.AxisListType.X

P = 128
D = 1024
KD = D // P
SEQ = 1024
NB, NQ, PAST = 8, 16, 128
T = SEQ + NB * NQ
TT = T // P
CH = 384
NC = T // CH
HD, H = 64, 8
PAIRS = H // 2
PASTS = NB * PAST
SB_Q, SB_K, SB_V = 0, 512, 1024
FX_Q, FX_K, FX_V, FX_F = 1536, 2048, 2560, 3072
NG, EG, NE, EH = 4, 4, 16, 256
SLOT_TILES = 34
SLOTS = SLOT_TILES * P
MASKED = -1.0e30
EPS = 1e-6
SHIFT1, SCALE1, GATE1, SHIFT2, SCALE2, GATE2 = (KD * n for n in range(6))


class Count:

    def __init__(self, sem, base=0):
        self.sem, self.base, self.n = sem, base, 0

    def inc(self, ins):
        ins.then_inc(self.sem, 1)
        self.n += 1
        return self.value()

    def value(self):
        return self.base + self.n

    def then_wait(self, eng, ins):
        eng.wait_ge(self.sem, self.inc(ins))


def program(nc, x_prompt, x_sample, cache_sb_k, cache_sb_v, cache_fox_k, cache_fox_v, cache_fox_logf,
            c_prompt, c_sample, w_ada, b_ada, g_mix, w_in, b_f, w_ba, w_bb, w_gate, b_gate, w_out,
            g_moe, w_rg, b_rg, w_re, b_re, w1, w3, w2, g_final,
            y_prompt, y_sample, sbk_p, sbv_p, fxk_p, fxv_p, lf_p, sbk_s, sbv_s, fxk_s, fxv_s, lf_s):
    scratch = lambda name, shape, dt=F32: nc.dram_tensor(name, shape, dt, kind="Internal").ap()
    xT_d = scratch("xT_d", (P, KD, T))
    y_d = scratch("y_d", (T, D))
    nf_d = scratch("nf_d", (H, SEQ + PASTS + P))
    mix_d = scratch("mix_d", (KD, P, T))
    x1_d = scratch("x1_d", (T, D))
    h2_d = scratch("h2_d", (T, D))
    slot_d = scratch("slot_d", (SLOTS, 1), I32)
    moe_d = scratch("moe_d", (SLOTS, D))

    top = ExitStack()

    def holder(ctx, stage):
        taken = []

        def give_back():
            nc.clear_and_free_semaphores(taken)
            nc.all_engine_barrier()

        def sem(name):
            taken.append(nc.alloc_semaphore(f"{stage}_{name}"))
            return taken[-1]

        if stage != "all":
            ctx.callback(give_back)
        sb = lambda name, shape, dt=F32: ctx.enter_context(nc.sbuf_tensor(f"{stage}_{name}", shape, dt))
        return sb, sem

    def cols(k, t):
        return slice(t * P, (t + 1) * P)

    with top:
        sb, sem = holder(top, "all")
        ident = sb("ident", [P, P])
        identb = sb("identb", [P, P], BF16)
        ones = sb("ones", [P, P])
        eps = sb("eps", [P, 1])
        vecT = sb("vecT", [P, 80])
        adaT = sb("adaT", [P, 48, 9])
        G = top.enter_context(nc.psum_tensor("G", [P, 6, 512], F32))
        TB = top.enter_context(nc.psum_tensor("TB", [P, 2, 512], F32))

        def stage_start(xT):
            ctx = ExitStack()
            with ctx:
                sb, sem = holder(ctx, "start")
                xrow = [sb(f"xrow{i}", [P, D]) for i in range(3)]
                crow = sb("crow", [9, D])
                csig = sb("csig", [9, D])
                vrow = sb("vrow", [80, P])
                cT = sb("cT", [P, KD, 9])
                wada = [sb(f"wada{i}", [P, KD, 512]) for i in range(2)]
                c_in, vec_in = sem("c_in"), sem("vec_in")
                x_in = [sem(f"x_in{i}") for i in range(3)]
                wada_in = [sem(f"wada_in{i}") for i in range(2)]
                consts, ident_ready = sem("consts"), sem("ident_ready")
                c_sig, c_ready, vec_turned, c_turned = sem("c_sig"), sem("c_ready"), sem("vec_turned"), sem("c_turned")
                cT_ready, x_turned, x_act, x_dve = sem("cT_ready"), sem("x_turned"), sem("x_act"), sem("x_dve")
                ada_done, ada_read, ada_vec, mod_step = sem("ada_done"), sem("ada_read"), sem("ada_vec"), sem("mod_step")
                block = ctx.enter_context(nc.Block())
                w_ada_v = w_ada[0].rearrange("(k p) n -> p k n", p=P)

                @block.sync
                def _(sp):
                    sp.dma_start(crow[0:1, :], c_prompt).then_inc(c_in, 16)
                    sp.dma_start(crow[1:9, :], c_sample).then_inc(c_in, 16)
                    sp.dma_start(vrow[0:48, :], b_ada[0].rearrange("(a n) -> a n", n=P)).then_inc(vec_in, 16)
                    sp.dma_start(vrow[48:56, :], g_mix[0].rearrange("(a n) -> a n", n=P)).then_inc(vec_in, 16)
                    sp.dma_start(vrow[56:64, :], g_moe[0].rearrange("(a n) -> a n", n=P)).then_inc(vec_in, 16)
                    sp.dma_start(vrow[64:80, :], b_gate[0].rearrange("(a n) -> a n", n=P)).then_inc(vec_in, 16)
                    for t in range(TT):
                        if t >= 3:
                            sp.wait_ge(x_turned, t - 2)
                        src = x_prompt[0, t * P:(t + 1) * P, :] if t < TT - 1 else x_sample.rearrange("b i n -> (b i) n")
                        sp.dma_start(xrow[t % 3][:], src).then_inc(x_in[t % 3], 16)
                        if t == 2:
                            for j in range(2):
                                sp.dma_start(wada[j][:], w_ada_v[:, :, j * 512:(j + 1) * 512]).then_inc(wada_in[j], 16)
                    with sp.Fori(0, 5) as i:
                        for j in range(2):
                            sp.wait_ge(ada_done, i * 2 + (j + 1))
                            sp.dma_start(wada[j][:], w_ada_v[:, :, bass.ds(i * 1024 + (j + 2) * 512, 512)])\
                              .then_inc(wada_in[j], 16)

                @block.gpsimd
                def _(pool):
                    pool.memset(ident[:], 0.0).then_inc(consts, 1)
                    pool.memset(ones[:], 1.0).then_inc(consts, 1)
                    pool.memset(eps[:], EPS).then_inc(consts, 1)
                    pool.wait_ge(consts, 3)
                    pool.affine_select(out=ident[:], in_=ident[:], compare_op=ALU.not_equal, fill=1.0, base=0,
                                       pattern=[[-1, P]], channel_multiplier=1).then_inc(ident_ready, 1)
                    pool.wait_ge(ident_ready, 1)
                    pool.tensor_copy(identb[:], ident[:]).then_inc(ident_ready, 1)

                @block.scalar
                def _(act):
                    act.wait_ge(c_in, 32)
                    act.activation(csig[:], crow[:], ACT.Sigmoid).then_inc(c_sig, 1)
                    for t in range(TT):
                        act.wait_ge(x_turned, t + 1)
                        act.activation(xT[:, 0:4, t * P:(t + 1) * P],
                                       G[:, 3 * (t % 2), :].rearrange("p (k n) -> p k n", n=P), ACT.Copy).then_inc(x_act, 1)

                @block.vector
                def _(dve):
                    dve.wait_ge(c_sig, 1)
                    dve.tensor_tensor(csig[:], csig[:], crow[:], ALU.mult).then_inc(c_ready, 1)
                    dve.wait_ge(vec_turned, 1)
                    dve.tensor_copy(vecT[:], TB[:, 0, 0:80]).then_inc(ada_vec, 1)
                    dve.wait_ge(c_turned, 1)
                    dve.tensor_copy(cT[:], TB[:, 1, 0:128].rearrange("p (k n) -> p k n", n=16)[:, :, 0:9]).then_inc(cT_ready, 1)
                    for t in range(TT):
                        dve.wait_ge(x_turned, t + 1)
                        dve.tensor_copy(xT[:, 4:8, t * P:(t + 1) * P],
                                        G[:, 3 * (t % 2) + 1, :].rearrange("p (k n) -> p k n", n=P)).then_inc(x_dve, 1)
                    dve.wait_ge(ada_vec, 1)
                    with dve.Fori(0, 6) as i:
                        for j in range(2):
                            dve.wait_ge(ada_done, i * 2 + (j + 1))
                            dve.tensor_tensor(adaT[:, bass.ds(i * 8 + 4 * j, 4), :],
                                              TB[:, j, :].rearrange("p (m n) -> p m n", n=P)[:, :, 0:9],
                                              vecT[:, bass.ds(i * 8 + 4 * j, 4)].unsqueeze(2).to_broadcast([P, 4, 9]),
                                              ALU.add).then_inc(ada_read, 1)
                    dve.wait_ge(ada_read, 12)
                    for scale, g in ((SCALE1, 48), (SCALE2, 56)):
                        dve.scalar_tensor_tensor(adaT[:, scale:scale + KD, :], adaT[:, scale:scale + KD, :], 1.0,
                                                 vecT[:, g:g + KD].unsqueeze(2).to_broadcast([P, KD, 9]),
                                                 ALU.add, ALU.mult).then_inc(mod_step, 1)

                @block.tensor
                def _(pe):
                    pe.wait_ge(ident_ready, 1)
                    pe.wait_ge(vec_in, 64)
                    pe.transpose(TB[:, 0, 0:80], vrow[:, :], ident[0:80, 0:80]).then_inc(vec_turned, 1)
                    pe.wait_ge(c_ready, 1)
                    for k in range(KD):
                        m = pe.transpose(TB[:, 1, k * 16:k * 16 + 9], csig[:, k * P:(k + 1) * P], ident[0:9, 0:9])
                    m.then_inc(c_turned, 1)
                    for t in range(TT):
                        pe.wait_ge(x_in[t % 3], 16 * (t // 3 + 1))
                        if t >= 2:
                            pe.wait_ge(x_act, t - 1)
                            pe.wait_ge(x_dve, t - 1)
                        for k in range(KD):
                            m = pe.transpose(G[:, 3 * (t % 2) + k // 4, (k % 4) * P:(k % 4 + 1) * P],
                                             xrow[t % 3][:, k * P:(k + 1) * P], ident[:])
                        m.then_inc(x_turned, 1)
                    pe.wait_ge(ada_vec, 1)
                    pe.wait_ge(cT_ready, 1)
                    with pe.Fori(0, 6) as i:
                        for j in range(2):
                            pe.wait_ge(wada_in[j], i * 16 + 16)
                            pe.wait_ge(ada_read, i * 2)
                            for m4 in range(4):
                                for k in range(KD):
                                    m = pe.matmul(TB[:, j, m4 * P:m4 * P + 9], wada[j][:, k, m4 * P:(m4 + 1) * P],
                                                  cT[:, k, :], start=k == 0, stop=k == KD - 1)
                            m.then_inc(ada_done, 1)

        def stage_norm(xT, scale, shift, hhi, hlo):
            ctx = ExitStack()
            with ctx:
                sb, sem = holder(ctx, "norm1" if hlo is not None else "norm2")
                sq = [sb(f"sq{i}", [P, CH]) for i in range(2)]
                rb = sb("rb", [P, T])
                tmp = [sb(f"tmp{i}", [P, T]) for i in range(2)]
                sq_ready, sq_used, root_ready, rstd_ready = sem("sq_ready"), sem("sq_used"), sem("root_ready"), sem("rstd_ready")
                normed, mod_sample, h_ready, hi_ready, lo_ready = sem("normed"), sem("mod_sample"), sem("h_ready"), sem("hi_ready"), sem("lo_ready")
                xT_out = sem("xT_out")
                block = ctx.enter_context(nc.Block())
                dst = (lambda k: tmp[k % 2][:]) if hlo is not None else (lambda k: hhi[:, k, :])

                if hlo is not None:
                    @block.sync
                    def _(sp):
                        sp.dma_start(xT_d, xT[:]).then_inc(xT_out, 16)
                        sp.wait_ge(xT_out, 16)

                @block.tensor
                def _(pe):
                    for c in range(NC):
                        for k in range(KD):
                            pe.wait_ge(sq_ready, c * KD + k + 1)
                            pe.matmul(G[:, c, 0:CH], ones[:], sq[k % 2][:], start=k == 0, stop=k == KD - 1).then_inc(sq_used, 1)

                @block.scalar
                def _(act):
                    for c in range(NC):
                        for k in range(KD):
                            n = c * KD + k
                            if n >= 2:
                                act.wait_ge(sq_used, n - 1)
                            act.activation(sq[k % 2][:], xT[:, k, c * CH:(c + 1) * CH], ACT.Square).then_inc(sq_ready, 1)
                    for c in range(NC):
                        act.wait_ge(sq_used, KD * (c + 1))
                        act.activation(rb[:, c * CH:(c + 1) * CH], G[:, c, 0:CH], ACT.Sqrt, bias=eps[:, 0:1],
                                       scale=1.0 / D).then_inc(root_ready, 1)
                    for k in range(KD):
                        act.wait_ge(normed, k + 1)
                        act.activation(dst(k)[:, 0:SEQ], dst(k)[:, 0:SEQ], ACT.Identity, bias=adaT[:, shift + k, 0:1],
                                       scale=adaT[:, scale + k, 0:1]).then_inc(h_ready, 1)
                        if hlo is not None:
                            act.wait_ge(h_ready, k + 1)
                            act.wait_ge(mod_sample, 2 * (k + 1))
                            act.activation(hhi[:, k, :], dst(k), ACT.Copy).then_inc(hi_ready, 1)

                @block.vector
                def _(dve):
                    for c in range(NC):
                        dve.wait_ge(root_ready, c + 1)
                        dve.reciprocal(rb[:, c * CH:(c + 1) * CH], rb[:, c * CH:(c + 1) * CH]).then_inc(rstd_ready, 1)
                    dve.wait_ge(rstd_ready, NC)

                    def low(k):
                        dve.wait_ge(hi_ready, k + 1)
                        dve.tensor_tensor(hlo[:, k, :], dst(k), hhi[:, k, :].bitcast(F32), ALU.subtract).then_inc(lo_ready, 1)

                    for k in range(KD):
                        if hlo is not None and k >= 2:
                            dve.wait_ge(lo_ready, k - 1)
                        dve.tensor_tensor(dst(k), xT[:, k, :], rb[:], ALU.mult).then_inc(normed, 1)
                        dve.wait_ge(normed, k + 1)
                        sample = dst(k)[:, SEQ:T].rearrange("p (b i) -> p b i", i=NQ)
                        for n, (row, op) in enumerate(((scale, ALU.mult), (shift, ALU.add))):
                            dve.tensor_tensor(sample, sample, adaT[:, row + k, 1:9].unsqueeze(2).to_broadcast([P, NB, NQ]),
                                              op).then_inc(mod_sample, 1)
                            dve.wait_ge(mod_sample, 2 * k + n + 1)
                        if hlo is not None and k >= 1:
                            low(k - 1)
                    if hlo is not None:
                        low(KD - 1)

        def stage_forget(hhi, hlo):
            ctx = ExitStack()
            with ctx:
                sb, sem = holder(ctx, "forget")
                wf = sb("wf", [P, KD, H])
                wfhi = sb("wfhi", [P, KD, P], F32R)
                wflo = sb("wflo", [P, KD, P], F32R)
                bf = sb("bf", [H, 1])
                z = sb("fz", [H, T])
                e = sb("fe", [H, T])
                lf = sb("lf", [H, T])
                nl = sb("nl", [H, T])
                cl = sb("cl", [H, PASTS])
                zero = sb("zero", [H, SEQ])
                nf = sb("nf", [H, SEQ + PASTS + P])
                wf_in, bf_in, cl_in = sem("wf_in"), sem("bf_in"), sem("cl_in")
                padded, wf_hi, wf_lo, fg_done, act_step, dve_step = (sem("padded"), sem("wf_hi"), sem("wf_lo"), sem("fg_done"),
                                                                     sem("f_act_step"), sem("f_dve_step"))
                e_ready, abs_ready, logf_ready, nf_ready = sem("e_ready"), sem("abs_ready"), sem("logf_ready"), sem("nf_ready")
                lf_out, nf_out = sem("lf_out"), sem("nf_out")
                block = ctx.enter_context(nc.Block())

                @block.sync
                def _(sp):
                    sp.dma_start(wf[:], w_in[0].rearrange("(k p) n -> p k n", p=P)[:, :, FX_F:FX_F + H]).then_inc(wf_in, 16)
                    sp.dma_start(bf[:], b_f.rearrange("a h -> h a")).then_inc(bf_in, 16)
                    sp.dma_start(cl[:].rearrange("h (b k) -> h b k", k=PAST),
                                 cache_fox_logf[0].rearrange("b h k -> h b k")).then_inc(cl_in, 16)
                    sp.wait_ge(logf_ready, 1)
                    sp.dma_start(lf_p[0, 0], lf[:, 0:SEQ]).then_inc(lf_out, 16)
                    sp.dma_start(lf_s[0].rearrange("b h i -> h b i"),
                                 lf[:, SEQ:T].rearrange("h (b i) -> h b i", i=NQ)).then_inc(lf_out, 16)
                    sp.wait_ge(nf_ready, 1)
                    sp.dma_start(nf_d, nf[:]).then_inc(nf_out, 16)
                    sp.wait_ge(lf_out, 32)
                    sp.wait_ge(nf_out, 16)

                @block.gpsimd
                def _(pool):
                    pool.memset(wfhi[:].bitcast(F32), 0.0).then_inc(padded, 1)
                    pool.memset(wflo[:].bitcast(F32), 0.0).then_inc(padded, 1)
                    pool.memset(zero[:], 0.0).then_inc(padded, 1)

                @block.scalar
                def _(act):
                    act.wait_ge(wf_in, 16)
                    act.wait_ge(padded, 3)
                    act.activation(wfhi[:, :, 0:H], wf[:], ACT.Copy).then_inc(wf_hi, 1)
                    act.wait_ge(bf_in, 16)
                    act.wait_ge(fg_done, 1)
                    step = Count(act_step)
                    step.then_wait(act, act.activation(z[:].rearrange("h (c n) -> h c n", n=CH), G[0:H, 0:NC, 0:CH],
                                                       ACT.Identity, bias=bf[:, 0:1]))
                    step.then_wait(act, act.activation(e[:], z[:], ACT.Abs))
                    step.then_wait(act, act.activation(e[:], e[:], ACT.Exp, scale=-1.0))
                    act.activation(e[:], e[:], ACT.Ln, bias=1.0).then_inc(e_ready, 1)

                @block.tensor
                def _(pe):
                    pe.wait_ge(wf_lo, 1)
                    for c in range(NC):
                        for k in range(KD):
                            for n, (w, h) in enumerate(((wfhi, hhi), (wfhi, hlo), (wflo, hhi))):
                                m = pe.matmul(G[:, c, 0:CH], w[:, k, :], h[:, k, c * CH:(c + 1) * CH],
                                              start=k == 0 and n == 0, stop=k == KD - 1 and n == 2)
                    m.then_inc(fg_done, 1)

                @block.vector
                def _(dve):
                    dve.wait_ge(wf_hi, 1)
                    dve.tensor_tensor(wflo[:, :, 0:H], wf[:], wfhi[:, :, 0:H].bitcast(F32), ALU.subtract).then_inc(wf_lo, 1)
                    step = Count(dve_step)
                    dve.wait_ge(e_ready, 1)
                    dve.scalar_tensor_tensor(lf[:], z[:], 0.0, e[:], ALU.min, ALU.subtract).then_inc(logf_ready, 1)
                    dve.wait_ge(logf_ready, 1)
                    step.then_wait(dve, dve.tensor_scalar(nl[:], lf[:], -1.0, None, ALU.mult))
                    dve.wait_ge(cl_in, 16)
                    step.then_wait(dve, dve.tensor_scalar(cl[:], cl[:], -1.0, None, ALU.mult))
                    step.inc(dve.tensor_tensor_scan(nf[:, 0:SEQ], nl[:, 0:SEQ], zero[:], 0.0, ALU.add, ALU.add))
                    for b in range(NB):
                        lo, new = SEQ + b * PAST, SEQ + PASTS + b * NQ
                        step.then_wait(dve, dve.tensor_tensor_scan(nf[:, lo:lo + PAST], cl[:, b * PAST:(b + 1) * PAST],
                                                                   zero[:, 0:PAST], 0.0, ALU.add, ALU.add))
                        step.inc(dve.tensor_tensor_scan(nf[:, new:new + NQ], nl[:, SEQ + b * NQ:SEQ + (b + 1) * NQ],
                                                        zero[:, 0:NQ], nf[:, lo + PAST - 1:lo + PAST], ALU.add, ALU.add))
                    dve.wait_ge(dve_step, step.value())
                    dve.tensor_copy(nf[:, 0:1], nf[:, 0:1]).then_inc(nf_ready, 1)

        def stage_attend(fox, hhi, hlo):
            ctx = ExitStack()
            QC, KC_, VC = (FX_Q, FX_K, FX_V) if fox else (SB_Q, SB_K, SB_V)
            cache_k, cache_v = (cache_fox_k[0], cache_fox_v[0]) if fox else (cache_sb_k[0], cache_sb_v[0])
            k_p, v_p, k_s, v_s = (fxk_p, fxv_p, fxk_s, fxv_s) if fox else (sbk_p, sbv_p, sbk_s, sbv_s)
            with ctx:
                sb, sem = holder(ctx, "fox" if fox else "sb")
                wraw = [sb(f"wraw{j}", [P, KD, P]) for j in range(2)]
                whi = [sb(f"whi{j}", [P, KD, P], F32R) for j in range(2)]
                wlo = [sb(f"wlo{j}", [P, KD, P], F32R) for j in range(2)]
                raw = [sb(f"raw{j}", [P, T]) for j in range(3)]
                qhi = [sb(f"qhi{h}", [P, T], F32R) for h in range(2)]
                qlo = [sb(f"qlo{h}", [P, T], F32R) for h in range(2)]
                ks = [sb(f"ks{h}", [P, T], F32R) for h in range(2)]
                kc = [sb(f"kc{h}", [P, PASTS], F32R) for h in range(2)]
                kcache = sb("kcache", [P, NB, P])
                vcache = sb("vcache", [P, NB, P])
                ktok = sb("ktok", [P, TT, P])
                vtok = sb("vtok", [P, TT, P])
                ytok = sb("ytok", [P, TT, P])
                S = [sb(f"S{i}", [P, T]) for i in range(2)]
                WT = [sb(f"WT{i}", [P, TT, P]) for i in range(2)]
                mdiag = sb("mdiag", [P, P], BF16)
                mnew = sb("mnew", [P, P], BF16)
                mpast = sb("mpast", [P, PASTS], BF16)
                if fox:
                    nfb = sb("nfb", [P, 2, SEQ + PASTS + P])
                    mx = sb("mx", [P, 2])
                    ssum = sb("ssum", [P, 2])
                else:
                    R = sb("R", [P, T])
                    SC = sb("SC", [P, T + 1])
                    zer = sb("zer", [P, 1])
                w_in_ = [sem(f"w_in{j}") for j in range(2)]
                kcache_in, vcache_in, nfb_in = sem("kcache_in"), sem("vcache_in"), sem("nfb_in")
                masks, w_hi, w_lo, proj_done, raw_ready = sem("masks"), sem("w_hi"), sem("w_lo"), sem("proj_done"), sem("raw_ready")
                q_hi, q_lo, k_hi, k_lo, kc_done, kc_hi, kc_lo = (sem("q_hi"), sem("q_lo"), sem("k_hi"), sem("k_lo"),
                                                                 sem("kc_done"), sem("kc_hi"), sem("kc_lo"))
                turned, t_dve, t_act = sem("turned"), sem("t_dve"), sem("t_act")
                z_ready, s_ready, r_ready, scanned, w_ready, pv_done, y_ready = (sem("z_ready"), sem("s_ready"), sem("r_ready"), sem("scanned"),
                                                                                 sem("w_ready"), sem("pv_done"), sem("y_ready"))
                max_ready, neg_ready, rinv_ready = sem("max_ready"), sem("neg_ready"), sem("rinv_ready")
                kv_out, y_out = sem("kv_out"), sem("y_out")
                waited_pool, waited_dve = sem("waited_pool"), sem("waited_dve")
                block = ctx.enter_context(nc.Block())
                w_v = w_in[0].rearrange("(k p) n -> p k n", p=P)
                items = [(h, t) for h in range(2) for t in range(TT)]
                NI = len(items)
                nblocks = lambda t: t + 1
                keys = lambda t: P * nblocks(t)
                uses = [(nblocks(t) + 3) // 4 for h, t in items]
                before = [sum(uses[:n]) for n in range(NI + 1)]
                KV_USES = 6
                TURNS = KV_USES + before[NI]
                assert TURNS % 2 == 0
                KV_OUT = 16 * 2 * (2 + NB)

                def zgroup(n):
                    return 3 * (n % 2)

                @block.gpsimd
                def _(pool):
                    pool.memset(mdiag[:], 0.0).then_inc(masks, 1)
                    pool.memset(mnew[:], 0.0).then_inc(masks, 1)
                    pool.memset(mpast[:], 0.0).then_inc(masks, 1)
                    step = Count(masks, 3)
                    pool.wait_ge(masks, 3)
                    strict = 0 if fox else -1
                    for m in (mdiag, mnew):
                        step.then_wait(pool, pool.affine_select(out=m[:], in_=m[:], compare_op=ALU.is_ge, fill=MASKED, base=strict,
                                                                pattern=[[-1, P]], channel_multiplier=1))
                    for m, n in ((mnew, NQ), (mpast, PAST)):
                        v = m[:].rearrange("p (b i) -> p b i", i=n)
                        step.then_wait(pool, pool.affine_select(out=v, in_=v, compare_op=ALU.is_ge, fill=MASKED, base=0,
                                                                pattern=[[-NQ, NB], [0, n]], channel_multiplier=1))
                        step.then_wait(pool, pool.affine_select(out=v, in_=v, compare_op=ALU.is_ge, fill=MASKED, base=NQ - 1,
                                                                pattern=[[NQ, NB], [0, n]], channel_multiplier=-1))
                    if not fox:
                        step.inc(pool.memset(zer[:], 0.0))
                        step.inc(pool.memset(SC[:, T:T + 1], 1.0))
                        with pool.Fori(0, PAIRS) as i:
                            for n, (h, t) in enumerate(items):
                                pool.wait_ge(s_ready, i * NI + (n + 1))
                                if n:
                                    pool.wait_ge(scanned, i * NI + n)
                                else:
                                    pool.wait_ge(scanned, i * NI)
                                pool.sem_inc(waited_pool)
                                pool.tensor_scalar(R[:, 0:keys(t)], S[n % 2][:, 0:keys(t)], -1.0, 1.0, ALU.mult, ALU.add)\
                                    .then_inc(r_ready, 1)
                MASKS = 9 + (0 if fox else 2)

                @block.sync
                def _(sp):
                    with sp.Fori(0, PAIRS) as i:
                        for j, col in enumerate((QC, KC_, VC)):
                            sp.wait_ge(w_lo, i * 3 + (1 if j == 2 else 0))
                            sp.dma_start(wraw[j % 2][:], w_v[:, :, bass.ds(i * P + col, P)]).then_inc(w_in_[j % 2], 16)
                        sp.wait_ge(pv_done, i * NI)
                        kv = cache_k.rearrange("b h k d -> k h b d")
                        vv = cache_v.rearrange("b h k d -> k h b d")
                        for h in range(2):
                            sp.dma_start(kcache[:, :, h * HD:(h + 1) * HD], kv[:, bass.ds(i * 2 + h, 1), :, :].rearrange("k a b d -> k (a b) d"))\
                              .then_inc(kcache_in, 16)
                            sp.dma_start(vcache[:, :, h * HD:(h + 1) * HD], vv[:, bass.ds(i * 2 + h, 1), :, :].rearrange("k a b d -> k (a b) d"))\
                              .then_inc(vcache_in, 16)
                        if fox:
                            for h in range(2):
                                sp.dma_start(nfb[:, h, :], nf_d[bass.ds(i * 2 + h, 1), :].to_broadcast([P, SEQ + PASTS + P]))\
                                  .then_inc(nfb_in, 16)
                        sp.wait_ge(t_dve, i * KV_USES + KV_USES)
                        for tok, o_p, o_s in ((ktok, k_p, k_s), (vtok, v_p, v_s)):
                            for h in range(2):
                                sp.dma_start(o_p[0, 0, bass.ds(i * 2 + h, 1)].rearrange("a (t p) d -> p (a t) d", p=P),
                                             tok[:, 0:TT - 1, h * HD:(h + 1) * HD]).then_inc(kv_out, 16)
                            for b in range(NB):
                                sp.dma_start(o_s[0, b, bass.ds(i * 2, 2)].rearrange("h q d -> q h d"),
                                             tok[b * NQ:(b + 1) * NQ, TT - 1, :].rearrange("q (h d) -> q h d", d=HD)).then_inc(kv_out, 16)
                        sp.wait_ge(y_ready, i * NI + NI)
                        sp.dma_start(y_d.rearrange("(t p) n -> p t n", p=P)[:, :, bass.ds(i * P + (512 if fox else 0), P)],
                                     ytok[:]).then_inc(y_out, 16)
                    sp.wait_ge(kv_out, PAIRS * KV_OUT)
                    sp.wait_ge(y_out, PAIRS * 16)

                @block.tensor
                def _(pe):
                    pe.wait_ge(masks, MASKS)
                    with pe.Fori(0, PAIRS) as i:
                        def project(j):
                            pe.wait_ge(w_lo, i * 3 + (j + 1))
                            if j == 2:
                                pe.wait_ge(raw_ready, i * 3 + 1)
                            elif j == 0:
                                pe.wait_ge(y_ready, i * NI)
                            g = 3 * (j % 2)
                            for k in range(KD):
                                for n, (w, hh) in enumerate(((whi, hhi), (whi, hlo), (wlo, hhi))):
                                    for c in range(NC):
                                        m = pe.matmul(G[:, g + c, 0:CH], w[j % 2][:, k, :], hh[:, k, c * CH:(c + 1) * CH],
                                                      start=k == 0 and n == 0, stop=k == KD - 1 and n == 2)
                            m.then_inc(proj_done, 1)

                        def bank_free(u):
                            if u < 2:
                                pe.wait_ge(t_act, i * before[NI])
                            elif u < KV_USES + 2:
                                pe.wait_ge(t_dve, i * KV_USES + (u - 1))
                            else:
                                pe.wait_ge(t_act, i * before[NI] + (u - KV_USES - 1))

                        def turn_kv(j, u0):
                            pe.wait_ge(raw_ready, i * 3 + (j + 1))
                            for u in range(3):
                                bank_free(u0 + u)
                                for b in range(4 * u, min(4 * u + 4, TT)):
                                    m = pe.transpose(TB[:, (u0 + u) % 2, (b % 4) * P:(b % 4 + 1) * P],
                                                     raw[j][:, b * P:(b + 1) * P], ident[:])
                                m.then_inc(turned, 1)

                        def scores(n):
                            h, t = items[n]
                            g = zgroup(n)
                            if n == 0:
                                pe.wait_ge(q_lo, i * 4 + 4)
                                pe.wait_ge(k_lo, i * 2 + 2)
                                pe.wait_ge(raw_ready, i * 3 + 3)
                            elif n == 1:
                                pe.wait_ge(kc_lo, i * 2 + 2)
                            else:
                                pe.wait_ge(y_ready, i * NI + (n - 1))
                            q = slice(t * P, (t + 1) * P)
                            if t < TT - 1:
                                parts = [(ks[h][:, lo:min(lo + 512, keys(t))], None) for lo in range(0, keys(t), 512)]
                                parts[-1] = (parts[-1][0], mdiag[:])
                            else:
                                parts = [(kc[h][:, lo:lo + 512], mpast[:, lo:lo + 512]) for lo in (0, 512)]
                                parts.append((ks[h][:, SEQ:T], mnew[:]))
                            for b, (key, mask) in enumerate(parts):
                                width = key.shape[1]
                                pe.matmul(G[:, g + b, 0:width], qhi[h][:, q], key, start=True, stop=False)
                                if mask is not None:
                                    mw = mask.shape[1]
                                    pe.matmul(G[:, g + b, width - mw:width], identb[:], mask, start=False, stop=False)
                                m = pe.matmul(G[:, g + b, 0:width], qlo[h][:, q], key, start=False, stop=True)
                            m.then_inc(z_ready, 1)

                        def turn_weights(n):
                            h, t = items[n]
                            pe.wait_ge(w_ready, i * NI + (n + 1))
                            for u in range(uses[n]):
                                use = KV_USES + before[n] + u
                                bank_free(use)
                                for b in range(4 * u, min(4 * u + 4, nblocks(t))):
                                    m = pe.transpose(TB[:, use % 2, (b % 4) * P:(b % 4 + 1) * P], S[n % 2][:, b * P:(b + 1) * P], ident[:])
                                m.then_inc(turned, 1)

                        def values(n):
                            h, t = items[n]
                            if n == 0:
                                pe.wait_ge(t_dve, i * KV_USES + KV_USES)
                            if n == TT - 1:
                                pe.wait_ge(vcache_in, i * 32 + 32)
                            out = G[:, zgroup(n) + 2, 256:256 + HD]
                            for b in range(nblocks(t)):
                                if b % 4 == 0:
                                    pe.wait_ge(t_act, i * before[NI] + (before[n] + b // 4 + 1))
                                src = vcache if t == TT - 1 and b < NB else vtok
                                m = pe.matmul(out, WT[n % 2][:, b, :], src[:, b, h * HD:(h + 1) * HD],
                                              start=b == 0, stop=b == nblocks(t) - 1)
                            m.then_inc(pv_done, 1)

                        project(0)
                        project(1)
                        project(2)
                        turn_kv(1, 0)
                        pe.wait_ge(kcache_in, i * 32 + 32)
                        for b in range(NB):
                            m = pe.transpose(G[:, 3 + b // 4, (b % 4) * P:(b % 4 + 1) * P], kcache[:, b, :], ident[:])
                        m.then_inc(kc_done, 1)
                        turn_kv(2, 3)
                        scores(0)
                        for n in range(NI):
                            if n + 1 < NI:
                                scores(n + 1)
                            turn_weights(n)
                            values(n)

                @block.scalar
                def _(act):
                    with act.Fori(0, PAIRS) as i:
                        def high(j):
                            act.wait_ge(w_in_[j % 2], i * 32 + 16 * (j // 2 + 1) if j % 2 == 0 else i * 16 + 16)
                            act.activation(whi[j % 2][:], wraw[j % 2][:], ACT.Copy).then_inc(w_hi, 1)

                        act.wait_ge(proj_done, i * 3)
                        high(0)
                        high(1)
                        for j in range(3):
                            act.wait_ge(proj_done, i * 3 + (j + 1))
                            if j == 0:
                                high(2)
                            act.activation(raw[j][:].rearrange("p (c n) -> p c n", n=CH), G[:, 3 * (j % 2):3 * (j % 2) + 3, 0:CH],
                                           ACT.Copy, scale=HD ** -0.5 if j == 0 else 1.0).then_inc(raw_ready, 1)
                            act.wait_ge(raw_ready, i * 3 + (j + 1))
                            if j == 0:
                                for h in range(2):
                                    for half in range(2):
                                        act.activation(qhi[h][half * HD:(half + 1) * HD, :], raw[0][h * HD:(h + 1) * HD, :], ACT.Copy).then_inc(q_hi, 1)
                            if j == 1:
                                for h in range(2):
                                    a = slice(h * HD, (h + 1) * HD)
                                    act.activation(ks[h][a, :], raw[1][a, :], ACT.Copy).then_inc(k_hi, 1)
                        act.wait_ge(kc_done, i + 1)
                        for h in range(2):
                            a = slice(h * HD, (h + 1) * HD)
                            act.activation(kc[h][a, :].rearrange("p (c n) -> p c n", n=512), G[a, 3:5, :], ACT.Copy).then_inc(kc_hi, 1)

                        def weigh(n):
                            h, t = items[n]
                            src = G[:, zgroup(n):zgroup(n) + 3, :].rearrange("p c n -> p (c n)")[:, 0:keys(t)]
                            if not fox:
                                act.wait_ge(z_ready, i * NI + (n + 1))
                                if n >= 2:
                                    act.wait_ge(turned, i * TURNS + (KV_USES + before[n - 1]))
                                act.activation(S[n % 2][:, 0:keys(t)], src, ACT.Sigmoid).then_inc(s_ready, 1)
                            else:
                                act.wait_ge(neg_ready, i * NI + (n + 1))
                                act.activation(S[n % 2][:, 0:keys(t)], S[n % 2][:, 0:keys(t)], ACT.Exp, bias=mx[:, n % 2:n % 2 + 1],
                                               accum_out=ssum[:, n % 2:n % 2 + 1]).then_inc(w_ready, 1)

                        def take_turned(n):
                            h, t = items[n]
                            if n >= 2:
                                act.wait_ge(pv_done, i * NI + (n - 1))
                            for u in range(uses[n]):
                                act.wait_ge(turned, i * TURNS + (KV_USES + before[n] + u + 1))
                                nb = min(4, nblocks(t) - 4 * u)
                                act.activation(WT[n % 2][:, 4 * u:4 * u + nb, :].rearrange("p b n -> p (b n)"),
                                               TB[:, (KV_USES + before[n] + u) % 2, 0:nb * P], ACT.Copy).then_inc(t_act, 1)

                        weigh(0)
                        for n in range(NI):
                            if n + 1 < NI:
                                weigh(n + 1)
                            take_turned(n)

                @block.vector
                def _(dve):
                    dve.wait_ge(masks, MASKS)
                    with dve.Fori(0, PAIRS) as i:
                        for j in range(3):
                            dve.wait_ge(w_hi, i * 3 + (j + 1))
                            dve.tensor_tensor(wlo[j % 2][:], wraw[j % 2][:], whi[j % 2][:].bitcast(F32), ALU.subtract).then_inc(w_lo, 1)
                        dve.wait_ge(q_hi, i * 4 + 4)
                        for h in range(2):
                            a = slice(h * HD, (h + 1) * HD)
                            for half in range(2):
                                dve.tensor_tensor(qlo[h][half * HD:(half + 1) * HD, :], raw[0][a, :], qhi[h][a, :].bitcast(F32),
                                                  ALU.subtract).then_inc(q_lo, 1)
                        dve.wait_ge(k_hi, i * 2 + 2)
                        for h in range(2):
                            a, o = slice(h * HD, (h + 1) * HD), slice((1 - h) * HD, (2 - h) * HD)
                            dve.tensor_tensor(ks[h][o, :], raw[1][a, :], ks[h][a, :].bitcast(F32), ALU.subtract).then_inc(k_lo, 1)

                        def take_kv(tok, u0):
                            if u0 == 0:
                                dve.wait_ge(kv_out, i * KV_OUT)
                            for u in range(3):
                                nb = min(4, TT - 4 * u)
                                dve.wait_ge(turned, i * TURNS + (u0 + u + 1))
                                dve.tensor_copy(tok[:, 4 * u:4 * u + nb, :].rearrange("p b n -> p (b n)"),
                                                TB[:, (u0 + u) % 2, 0:nb * P]).then_inc(t_dve, 1)

                        take_kv(ktok, 0)
                        dve.wait_ge(kc_hi, i * 2 + 2)
                        for h in range(2):
                            a, o = slice(h * HD, (h + 1) * HD), slice((1 - h) * HD, (2 - h) * HD)
                            dve.tensor_tensor(kc[h][o, :].rearrange("p (c n) -> p c n", n=512), G[a, 3:5, :],
                                              kc[h][a, :].bitcast(F32).rearrange("p (c n) -> p c n", n=512),
                                              ALU.subtract).then_inc(kc_lo, 1)
                        take_kv(vtok, 3)
                        if fox:
                            dve.wait_ge(nfb_in, i * 32 + 32)
                        dve.wait_ge(y_out, i * 16)

                        def weigh(n):
                            h, t = items[n]
                            w = keys(t)
                            if fox:
                                src = G[:, zgroup(n):zgroup(n) + 3, :].rearrange("p c n -> p (c n)")[:, 0:w]
                                f = nfb[:, h, 0:w] if t < TT - 1 else nfb[:, h, SEQ:SEQ + w]
                                dve.wait_ge(z_ready, i * NI + (n + 1))
                                if n >= 2:
                                    dve.wait_ge(turned, i * TURNS + (KV_USES + before[n - 1]))
                                dve.sem_inc(waited_dve)
                                dve.tensor_tensor_reduce(out=S[n % 2][:, 0:w], in0=src, in1=f, scale=1.0, scalar=-3.0e38,
                                                         op0=ALU.add, op1=ALU.max, accum_out=mx[:, n % 2:n % 2 + 1]).then_inc(max_ready, 1)
                                dve.wait_ge(max_ready, i * NI + (n + 1))
                                dve.tensor_scalar(mx[:, n % 2:n % 2 + 1], mx[:, n % 2:n % 2 + 1], -1.0, None, ALU.mult).then_inc(neg_ready, 1)
                            else:
                                dve.wait_ge(r_ready, i * NI + (n + 1))
                                lo = T - w
                                back = SC[:, lo:T][:, ::-1]
                                dve.wait_ge(w_ready, i * NI + n)
                                dve.tensor_tensor_scan(back, R[:, 0:w][:, ::-1], zer[:, 0:1].to_broadcast([P, w]), 1.0, ALU.mult, ALU.add).then_inc(scanned, 1)
                                dve.wait_ge(scanned, i * NI + (n + 1))
                                dve.tensor_tensor(S[n % 2][:, 0:w], S[n % 2][:, 0:w], SC[:, lo + 1:T + 1], ALU.mult).then_inc(w_ready, 1)

                        def finish(n):
                            h, t = items[n]
                            out, src = ytok[:, t, h * HD:(h + 1) * HD], G[:, zgroup(n) + 2, 256:256 + HD]
                            if fox:
                                dve.wait_ge(w_ready, i * NI + (n + 1))
                                dve.reciprocal(ssum[:, n % 2:n % 2 + 1], ssum[:, n % 2:n % 2 + 1]).then_inc(rinv_ready, 1)
                                dve.wait_ge(rinv_ready, i * NI + (n + 1))
                                dve.wait_ge(pv_done, i * NI + (n + 1))
                                dve.tensor_scalar(out, src, ssum[:, n % 2:n % 2 + 1], None, ALU.mult).then_inc(y_ready, 1)
                            else:
                                dve.wait_ge(pv_done, i * NI + (n + 1))
                                dve.tensor_copy(out, src).then_inc(y_ready, 1)

                        weigh(0)
                        for n in range(NI):
                            if n + 1 < NI:
                                weigh(n + 1)
                            finish(n)

        def stage_turn_y(yhi, ylo):
            ctx = ExitStack()
            with ctx:
                sb, sem = holder(ctx, "turn_y")
                yrow = [sb(f"yrow{i}", [P, D]) for i in range(3)]
                yrow_in = [sem(f"yrow_in{i}") for i in range(3)]
                y_turned, y_hi, y_lo = sem("y_turned"), sem("y_hi"), sem("y_lo")
                block = ctx.enter_context(nc.Block())

                def banks(t):
                    return G[:, 3 * (t % 2):3 * (t % 2) + 2, :].rearrange("p c (k n) -> p (c k) n", n=P)

                @block.sync
                def _(sp):
                    for t in range(TT):
                        if t >= 3:
                            sp.wait_ge(y_turned, t - 2)
                        sp.dma_start(yrow[t % 3][:], y_d[t * P:(t + 1) * P, :]).then_inc(yrow_in[t % 3], 16)

                @block.tensor
                def _(pe):
                    for t in range(TT):
                        pe.wait_ge(yrow_in[t % 3], 16 * (t // 3 + 1))
                        if t >= 2:
                            pe.wait_ge(y_lo, t - 1)
                        for k in range(KD):
                            m = pe.transpose(banks(t)[:, k, :], yrow[t % 3][:, k * P:(k + 1) * P], ident[:])
                        m.then_inc(y_turned, 1)

                @block.scalar
                def _(act):
                    for t in range(TT):
                        act.wait_ge(y_turned, t + 1)
                        act.activation(yhi[:, :, t * P:(t + 1) * P], banks(t), ACT.Copy).then_inc(y_hi, 1)

                @block.vector
                def _(dve):
                    for t in range(TT):
                        dve.wait_ge(y_hi, t + 1)
                        dve.tensor_tensor(ylo[:, :, t * P:(t + 1) * P], banks(t), yhi[:, :, t * P:(t + 1) * P].bitcast(F32),
                                          ALU.subtract).then_inc(y_lo, 1)

        def stage_merge(hhi, hlo, yhi, ylo):
            ctx = ExitStack()
            with ctx:
                sb, sem = holder(ctx, "merge")
                kn = (KD, 4, KD, 4)
                wraw = [sb(f"mraw{j}", [P, kn[j], P]) for j in range(4)]
                whi = [sb(f"mhi{j}", [P, kn[j], P], F32R) for j in range(4)]
                wlo = [sb(f"mlo{j}", [P, kn[j], P], F32R) for j in range(4)]
                sg = [sb(f"sg{j}", [P, T]) for j in range(2)]
                w_in_ = [sem(f"mw_in{j}") for j in range(4)]
                w_hi, w_lo, prod_done, sg_ready, m_ready, mix_ready, mix_out = (sem("mw_hi"), sem("mw_lo"), sem("prod_done"), sem("sg_ready"),
                                                                                sem("m_ready"), sem("mix_ready"), sem("mix_out"))
                block = ctx.enter_context(nc.Block())
                wg = w_gate[0].rearrange("(k p) n -> p k n", p=P)
                srcs = (wg[:, :, 0:D], w_ba[0].rearrange("(k p) n -> p k n", p=P), wg[:, :, D:2 * D],
                        w_bb[0].rearrange("(k p) n -> p k n", p=P))

                @block.sync
                def _(sp):
                    with sp.Fori(0, KD) as i:
                        for j in range(4):
                            sp.wait_ge(w_lo, i * 4)
                            sp.dma_start(wraw[j][:], srcs[j][:, :, bass.ds(i * P, P)]).then_inc(w_in_[j], 16)
                        sp.wait_ge(mix_ready, i + 1)
                        sp.dma_start(mix_d[bass.ds(i, 1)].rearrange("a p n -> (a p) n"), sg[0][:]).then_inc(mix_out, 16)
                    sp.wait_ge(mix_out, 16 * KD)

                @block.tensor
                def _(pe):
                    with pe.Fori(0, KD) as i:
                        for j in range(4):
                            pe.wait_ge(w_lo, i * 4 + (j + 1))
                            pe.wait_ge(sg_ready if j % 2 == 0 else m_ready, i * 2 + j // 2)
                            g = 3 * (j % 2)
                            hi, lo, k0 = (hhi, hlo, 0) if j % 2 == 0 else (yhi, ylo, 4 * (j // 2))
                            for k in range(kn[j]):
                                for n, (w, a) in enumerate(((whi, hi), (whi, lo), (wlo, hi))):
                                    for c in range(NC):
                                        m = pe.matmul(G[:, g + c, 0:CH], w[j][:, k, :], a[:, k0 + k, c * CH:(c + 1) * CH],
                                                      start=k == 0 and n == 0, stop=k == kn[j] - 1 and n == 2)
                            m.then_inc(prod_done, 1)

                @block.scalar
                def _(act):
                    with act.Fori(0, KD) as i:
                        for j in range(4):
                            act.wait_ge(w_in_[j], i * 16 + 16)
                            if j == 0:
                                act.wait_ge(prod_done, i * 4)
                            act.activation(whi[j][:], wraw[j][:], ACT.Copy).then_inc(w_hi, 1)
                        for j in range(2):
                            act.wait_ge(prod_done, i * 4 + (2 * j + 1))
                            if j == 0:
                                act.wait_ge(mix_out, i * 16)
                            act.activation(sg[j][:].rearrange("p (c n) -> p c n", n=CH), G[:, 0:3, 0:CH], ACT.Sigmoid,
                                           bias=vecT[:, bass.ds(i + (64 + 8 * j), 1)]).then_inc(sg_ready, 1)

                @block.vector
                def _(dve):
                    with dve.Fori(0, KD) as i:
                        for j in range(4):
                            dve.wait_ge(w_hi, i * 4 + (j + 1))
                            dve.tensor_tensor(wlo[j][:], wraw[j][:], whi[j][:].bitcast(F32), ALU.subtract).then_inc(w_lo, 1)
                        for j in range(2):
                            dve.wait_ge(sg_ready, i * 2 + (j + 1))
                            dve.wait_ge(prod_done, i * 4 + (2 * j + 2))
                            v = sg[j][:].rearrange("p (c n) -> p c n", n=CH)
                            dve.tensor_tensor(v, G[:, 3:6, 0:CH], v, ALU.mult).then_inc(m_ready, 1)
                        dve.wait_ge(m_ready, i * 2 + 2)
                        dve.tensor_tensor(sg[0][:], sg[0][:], sg[1][:], ALU.add).then_inc(mix_ready, 1)

        def stage_out(xT):
            ctx = ExitStack()
            with ctx:
                sb, sem = holder(ctx, "out")
                mraw = [sb(f"xraw{j}", [P, T]) for j in range(2)]
                mhi = sb("mixhi", [P, KD, T], F32R)
                mlo = sb("mixlo", [P, KD, T], F32R)
                wraw = [sb(f"oraw{j}", [P, KD, P]) for j in range(2)]
                whi = [sb(f"ohi{j}", [P, KD, P], F32R) for j in range(2)]
                wlo = [sb(f"olo{j}", [P, KD, P], F32R) for j in range(2)]
                tmp = sb("otmp", [P, P])
                mix_in = [sem(f"mix_in{j}") for j in range(2)]
                w_in_ = [sem(f"ow_in{j}") for j in range(2)]
                xT_in, m_hi, m_lo, w_hi, w_lo, prod_done, step_s, out_ready = (sem("xT_in"), sem("m_hi"), sem("m_lo"), sem("ow_hi"), sem("ow_lo"),
                                                                               sem("oprod_done"), sem("ostep"), sem("out_ready"))
                block = ctx.enter_context(nc.Block())
                wv = w_out[0].rearrange("(k p) n -> p k n", p=P)

                @block.sync
                def _(sp):
                    for k in range(KD):
                        if k >= 2:
                            sp.wait_ge(m_lo, k - 1)
                        sp.dma_start(mraw[k % 2][:], mix_d[k]).then_inc(mix_in[k % 2], 16)
                    sp.dma_start(xT[:], xT_d).then_inc(xT_in, 16)
                    with sp.Fori(0, KD // 2) as i:
                        for j in range(2):
                            sp.wait_ge(w_lo, i * 2)
                            sp.dma_start(wraw[j][:], wv[:, :, bass.ds(i * 2 * P + j * P, P)]).then_inc(w_in_[j], 16)

                @block.tensor
                def _(pe):
                    pe.wait_ge(m_lo, KD)
                    with pe.Fori(0, KD // 2) as i:
                        for j in range(2):
                            pe.wait_ge(w_lo, i * 2 + (j + 1))
                            pe.wait_ge(out_ready, i * 2)
                            for k in range(KD):
                                for n, (w, a) in enumerate(((whi, mhi), (whi, mlo), (wlo, mhi))):
                                    for c in range(NC):
                                        m = pe.matmul(G[:, 3 * j + c, 0:CH], w[j][:, k, :], a[:, k, c * CH:(c + 1) * CH],
                                                      start=k == 0 and n == 0, stop=k == KD - 1 and n == 2)
                            m.then_inc(prod_done, 1)

                @block.scalar
                def _(act):
                    for k in range(KD):
                        act.wait_ge(mix_in[k % 2], 16 * (k // 2 + 1))
                        act.activation(mhi[:, k, :], mraw[k % 2][:], ACT.Copy).then_inc(m_hi, 1)
                    with act.Fori(0, KD // 2) as i:
                        for j in range(2):
                            act.wait_ge(w_in_[j], i * 16 + 16)
                            act.wait_ge(prod_done, i * 2)
                            act.activation(whi[j][:], wraw[j][:], ACT.Copy).then_inc(w_hi, 1)

                @block.vector
                def _(dve):
                    for k in range(KD):
                        dve.wait_ge(m_hi, k + 1)
                        dve.tensor_tensor(mlo[:, k, :], mraw[k % 2][:], mhi[:, k, :].bitcast(F32), ALU.subtract).then_inc(m_lo, 1)
                    dve.wait_ge(xT_in, 16)
                    with dve.Fori(0, KD // 2) as i:
                        step = Count(step_s, i * 2)
                        for j in range(2):
                            dve.wait_ge(w_hi, i * 2 + (j + 1))
                            dve.tensor_tensor(wlo[j][:], wraw[j][:], whi[j][:].bitcast(F32), ALU.subtract).then_inc(w_lo, 1)
                        for j in range(2):
                            dve.wait_ge(prod_done, i * 2 + (j + 1))
                            row = lambda lo, n: xT[:, bass.ds(i * 2 + j, 1), lo:lo + n].rearrange("p a n -> p (a n)")
                            gate = lambda lo, n: adaT[:, bass.ds(i * 2 + (GATE1 + j), 1), lo:lo + n].rearrange("p a n -> p (a n)")
                            g = 3 * j
                            dve.wait_ge(out_ready, i * 2 + j)
                            step.then_wait(dve, dve.tensor_tensor(tmp[:].rearrange("p (b q) -> p b q", q=NQ),
                                                                  G[:, g + 2, 256:CH].rearrange("p (b q) -> p b q", q=NQ),
                                                                  gate(1, NB).unsqueeze(2).to_broadcast([P, NB, NQ]), ALU.mult))
                            dve.tensor_tensor(row(SEQ, P), row(SEQ, P), tmp[:], ALU.add)
                            dve.scalar_tensor_tensor(row(0, 2 * CH).rearrange("p (c n) -> p c n", n=CH), G[:, g:g + 2, 0:CH], gate(0, 1),
                                                     row(0, 2 * CH).rearrange("p (c n) -> p c n", n=CH), ALU.mult, ALU.add)
                            dve.scalar_tensor_tensor(row(2 * CH, 256), G[:, g + 2, 0:256], gate(0, 1), row(2 * CH, 256),
                                                     ALU.mult, ALU.add).then_inc(out_ready, 1)

        def stage_route(xT, h2T, slots, weights, tile_expert):
            ctx = ExitStack()
            with ctx:
                sb, sem = holder(ctx, "route")
                rows = [sb(f"rows{i}", [P, D]) for i in range(2)]
                wr = sb("wr", [P, KD, NG + NE])
                bias = sb("bias", [P, NG + NE])
                L = sb("L", [P, TT, NG + NE])
                w4 = sb("w4", [P, 4])
                tri = sb("tri", [P, P])
                jl = sb("jl", [P, SLOT_TILES])
                ids = sb("ids", [P, TT], I32)
                zslot = sb("zslot", [P, SLOT_TILES], I32)
                sl_i = slots
                f9 = lambda name, *s: sb(name, [P, TT, *s])
                gmax, geq, oh_g, prod16, esel = f9("gmax"), f9("geq", 4), f9("oh_g", 4), f9("prod16", 4, 4), f9("esel", 4)
                m1, m2, oh1, oh2, e2, gsum = f9("m1"), f9("m2"), f9("oh1", 4), f9("oh2", 4), f9("e2", 4), f9("gsum")
                X1, X2, M, DD = f9("X1", 4, 4), f9("X2", 4, 4), f9("M", NE), f9("DD", NE)
                off = sb("off", [P, TT + 1, NE])
                cnt = sb("cnt", [P, NE])
                cnt_i = sb("cnt_i", [P, NE], I32)
                ends = sb("ends", [P, NE])
                zero16 = sb("zero16", [P, NE])
                cmp = sb("cmp", [P, SLOT_TILES, NE])
                te = sb("te", [P, SLOT_TILES])
                sl = sb("sl", [P, 2, TT])
                sl_p = sb("sl_p", [P, 2 * TT], I32)
                sl_j = sb("sl_j", [P, 2 * TT], I32)
                wr_in, bias_in, consts, turned, r_act, r_dve = (sem("wr_in"), sem("bias_in"), sem("rconsts"), sem("rturned"), sem("r_act"), sem("r_dve"))
                row_out = [sem(f"row_out{i}") for i in range(2)]
                logits, dve_step, exp_in, exp_out, exp2_in, exp2_out = (sem("logits"), sem("rdve_step"), sem("exp_in"), sem("exp_out"),
                                                                        sem("exp2_in"), sem("exp2_out"))
                m_ready, prefix, slots_ready, cleared, put = sem("rm_ready"), sem("prefix"), sem("slots_ready"), sem("cleared"), sem("put")
                block = ctx.enter_context(nc.Block())
                jobs = [(src, dst, t) for t in range(TT) for src, dst in ((xT, x1_d), (h2T, h2_d))]

                @block.sync
                def _(sp):
                    wv = wr[:]
                    sp.dma_start(wv[:, :, 0:NG], w_rg[0].rearrange("(k p) n -> p k n", p=P)).then_inc(wr_in, 16)
                    sp.dma_start(wv[:, :, NG:NG + NE], w_re[0].rearrange("(k p) n -> p k n", p=P)).then_inc(wr_in, 16)
                    sp.dma_start(bias[:, 0:NG], b_rg.to_broadcast([P, NG])).then_inc(bias_in, 16)
                    sp.dma_start(bias[:, NG:NG + NE], b_re.to_broadcast([P, NE])).then_inc(bias_in, 16)
                    for n, (src, dst, t) in enumerate(jobs):
                        sp.wait_ge(r_act, n + 1)
                        sp.wait_ge(r_dve, n + 1)
                        sp.dma_start(dst[t * P:(t + 1) * P, :], rows[n % 2][:]).then_inc(row_out[n % 2], 16)
                    for n in range(2):
                        sp.wait_ge(row_out[n], 16 * TT)

                @block.gpsimd
                def _(pool):
                    step = Count(consts)
                    step.inc(pool.memset(tri[:], 0.0))
                    step.inc(pool.memset(zero16[:], 0.0))
                    step.inc(pool.memset(off[:, 0, :], 0.0))
                    step.inc(pool.memset(zslot[:], 0))
                    step.inc(pool.iota(w4[:], [[-1, 4]], base=4, channel_multiplier=0, allow_small_or_imprecise_dtypes=True))
                    step.inc(pool.iota(jl[:], [[1, SLOT_TILES]], base=0, channel_multiplier=0, allow_small_or_imprecise_dtypes=True))
                    step.then_wait(pool, pool.iota(ids[:], [[P, TT]], base=0, channel_multiplier=1))
                    step.inc(pool.affine_select(out=tri[:], in_=tri[:], compare_op=ALU.is_ge, fill=1.0, base=0,
                                                pattern=[[-1, P]], channel_multiplier=1))
                    pool.dma_start(slot_d.rearrange("(p j) a -> p (j a)", p=P), zslot[:]).then_inc(cleared, 16)
                    pool.wait_ge(cleared, 16)
                    pool.wait_ge(slots_ready, 1)
                    for c in range(2):
                        for t in range(TT):
                            pool.indirect_dma_start(slot_d, bass.IndirectOffsetOnAxis(ap=sl_i[:, c * TT + t:c * TT + t + 1], axis=0),
                                                    ids[:, t:t + 1], None).then_inc(put, 16)
                    pool.wait_ge(put, 16 * 2 * TT)

                @block.tensor
                def _(pe):
                    pe.wait_ge(wr_in, 32)
                    for t in range(TT):
                        for k in range(KD):
                            m = pe.matmul(TB[:, 0, t * 32:t * 32 + NG + NE], h2T[:, k, t * P:(t + 1) * P], wr[:, k, :],
                                          start=k == 0, stop=k == KD - 1)
                    m.then_inc(logits, 1)
                    for n, (src, dst, t) in enumerate(jobs):
                        if n >= 2:
                            pe.wait_ge(r_act, n - 1)
                            pe.wait_ge(r_dve, n - 1)
                        for k in range(KD):
                            m = pe.transpose(G[:, 3 * (n % 2) + k // 4, (k % 4) * P:(k % 4 + 1) * P], src[:, k, t * P:(t + 1) * P], ident[:])
                        m.then_inc(turned, 1)
                        if n == 3:
                            pe.wait_ge(consts, 8)
                            pe.wait_ge(m_ready, 1)
                            pe.matmul(TB[:, 1, 0:TT * NE], tri[:], M[:].rearrange("p t e -> p (t e)"), start=True, stop=True)
                            pe.matmul(TB[:, 1, 256:256 + TT * NE], ones[:], M[:].rearrange("p t e -> p (t e)"), start=True, stop=True)\
                              .then_inc(prefix, 1)

                def take(eng, n, half, copy, done):
                    eng.wait_ge(turned, n + 1)
                    if n >= 2:
                        eng.wait_ge(row_out[n % 2], 16 * (n // 2))
                    copy(rows[n % 2][:, half * 512:(half + 1) * 512], G[:, 3 * (n % 2) + half, :]).then_inc(done, 1)

                @block.scalar
                def _(act):
                    for s_in, s_out, v in ((exp_in, exp_out, geq[:]), (exp2_in, exp2_out, m2[:])):
                        act.wait_ge(s_in, 1)
                        act.activation(v, v, ACT.Exp).then_inc(s_out, 1)
                    for n in range(len(jobs)):
                        take(act, n, 0, lambda o, i: act.activation(o, i, ACT.Copy), r_act)

                @block.vector
                def _(dve):
                    step = Count(dve_step)

                    def do(ins):
                        step.then_wait(dve, ins)

                    def over4(v):
                        return v.unsqueeze(2).to_broadcast([P, TT, 4])

                    def first_max(oh, v, m, t4):
                        do(dve.tensor_reduce(m, v, AX, ALU.max))
                        do(dve.tensor_tensor(oh, v, over4(m), ALU.is_equal))
                        do(dve.tensor_tensor(oh, oh, w4[:].unsqueeze(1).to_broadcast([P, TT, 4]), ALU.mult))
                        do(dve.tensor_reduce(t4, oh, AX, ALU.max))
                        do(dve.tensor_tensor(oh, oh, over4(t4), ALU.is_equal))

                    dve.wait_ge(consts, 8)
                    dve.wait_ge(bias_in, 32)
                    dve.wait_ge(logits, 1)
                    do(dve.tensor_tensor(L[:], TB[:, 0, 0:TT * 32].rearrange("p (t n) -> p t n", n=32)[:, :, 0:NG + NE],
                                         bias[:].unsqueeze(1).to_broadcast([P, TT, NG + NE]), ALU.add))
                    g = L[:, :, 0:NG]
                    first_max(oh_g[:], g, gmax[:], gsum[:])
                    dve.tensor_tensor(geq[:], g, over4(gmax[:]), ALU.subtract).then_inc(exp_in, 1)
                    e44 = L[:, :, NG:NG + NE].rearrange("p t (g j) -> p t g j", j=EG)
                    do(dve.tensor_tensor(prod16[:], e44, oh_g[:].unsqueeze(3).to_broadcast([P, TT, 4, 4]), ALU.mult))
                    do(dve.tensor_reduce(esel[:], prod16[:].rearrange("p t g j -> p t j g"), AX, ALU.add))
                    first_max(oh1[:], esel[:], m1[:], gmax[:])
                    do(dve.scalar_tensor_tensor(e2[:], oh1[:], -3.0e38, esel[:], ALU.mult, ALU.add))
                    first_max(oh2[:], e2[:], m2[:], gmax[:])
                    dve.tensor_tensor(m2[:], m2[:], m1[:], ALU.subtract).then_inc(exp2_in, 1)
                    for X, oh in ((X1, oh1), (X2, oh2)):
                        do(dve.tensor_tensor(X[:], oh_g[:].unsqueeze(3).to_broadcast([P, TT, 4, 4]),
                                             oh[:].unsqueeze(2).to_broadcast([P, TT, 4, 4]), ALU.mult))
                    flat = lambda X: X[:].rearrange("p t g j -> p t (g j)")
                    dve.tensor_tensor(M[:], flat(X1), flat(X2), ALU.add).then_inc(m_ready, 1)
                    dve.wait_ge(exp_out, 1)
                    do(dve.tensor_reduce(gsum[:], geq[:], AX, ALU.add))
                    dve.wait_ge(exp2_out, 1)
                    do(dve.tensor_scalar(m1[:], m2[:], 1.0, None, ALU.add))
                    do(dve.tensor_tensor(m1[:], m1[:], gsum[:], ALU.mult))
                    do(dve.reciprocal(weights[:, 0, :], m1[:]))
                    do(dve.tensor_tensor(weights[:, 1, :], weights[:, 0, :], m2[:], ALU.mult))
                    for n in range(4):
                        take(dve, n, 1, lambda o, i: dve.tensor_copy(o, i), r_dve)
                    dve.wait_ge(prefix, 1)
                    for t in range(TT):
                        do(dve.tensor_tensor(off[:, t + 1, :], off[:, t, :], TB[:, 1, 256 + t * NE:256 + (t + 1) * NE], ALU.add))
                    do(dve.tensor_scalar(cnt[:], off[:, TT, :], float(P - 1), None, ALU.add))
                    do(dve.tensor_copy(cnt_i[:], cnt[:]))
                    do(dve.tensor_scalar(cnt_i[:], cnt_i[:], 7, None, ALU.arith_shift_right))
                    do(dve.tensor_copy(cnt[:], cnt_i[:]))
                    do(dve.tensor_tensor_scan(ends[:], cnt[:], zero16[:], 0.0, ALU.add, ALU.add))
                    do(dve.tensor_tensor(cnt[:], ends[:], cnt[:], ALU.subtract))
                    do(dve.tensor_tensor(DD[:], TB[:, 1, 0:TT * NE].rearrange("p (t e) -> p t e", e=NE), off[:, 0:TT, :], ALU.add))
                    do(dve.scalar_tensor_tensor(DD[:], cnt[:].unsqueeze(1).to_broadcast([P, TT, NE]), float(P), DD[:], ALU.mult, ALU.add))
                    for c, X in enumerate((X1, X2)):
                        do(dve.tensor_tensor(flat(X), flat(X), DD[:], ALU.mult))
                        do(dve.tensor_reduce(sl[:, c, :], flat(X), AX, ALU.add))
                    do(dve.tensor_copy(sl_p[:], sl[:].rearrange("p c t -> p (c t)")))
                    do(dve.tensor_scalar(sl_j[:], sl_p[:], 7, None, ALU.arith_shift_right))
                    do(dve.tensor_scalar(sl_p[:], sl_p[:], P - 1, None, ALU.bitwise_and))
                    dve.scalar_tensor_tensor(sl_i[:], sl_p[:], float(SLOT_TILES), sl_j[:], ALU.mult, ALU.add).then_inc(slots_ready, 1)
                    do(dve.tensor_tensor(cmp[:], ends[:].unsqueeze(1).to_broadcast([P, SLOT_TILES, NE]),
                                         jl[:].unsqueeze(2).to_broadcast([P, SLOT_TILES, NE]), ALU.is_le))
                    do(dve.tensor_reduce(te[:], cmp[:], AX, ALU.add))
                    do(dve.tensor_scalar(te[:], te[:], float(NE - 1), None, ALU.min))
                    do(dve.tensor_copy(tile_expert[:], te[:]))
                    for n in range(4, len(jobs)):
                        take(dve, n, 1, lambda o, i: dve.tensor_copy(o, i), r_dve)

        def stage_experts(tile_expert):
            ctx = ExitStack()
            with ctx:
                sb, sem = holder(ctx, "experts")
                tok = sb("tok", [P, SLOT_TILES], I32)
                idx = [sb(f"idx{j}", [P, 1], I32) for j in range(2)]
                hg = [sb(f"hg{j}", [P, D]) for j in range(2)]
                ghi = [sb(f"ghi{j}", [P, KD, P], F32R) for j in range(2)]
                glo = [sb(f"glo{j}", [P, KD, P], F32R) for j in range(2)]
                ur = [sb(f"ur{j}", [P, KD, 2 * EH]) for j in range(2)]
                uhi = [sb(f"uhi{j}", [P, KD, 2 * EH], F32R) for j in range(2)]
                ulo = [sb(f"ulo{j}", [P, KD, 2 * EH], F32R) for j in range(2)]
                dr = [sb(f"dr{j}", [P, 2, D]) for j in range(2)]
                dhi = [sb(f"dhi{j}", [P, 2, D], F32R) for j in range(2)]
                dlo = [sb(f"dlo{j}", [P, 2, D], F32R) for j in range(2)]
                sg = [sb(f"esg{j}", [P, EH]) for j in range(2)]
                ahi = [sb(f"ahi{j}", [P, 2, P], F32R) for j in range(2)]
                alo = [sb(f"alo{j}", [P, 2, P], F32R) for j in range(2)]
                yo = [sb(f"yo{j}", [P, D]) for j in range(2)]
                tok_in, waited_pool = sem("tok_in"), sem("waited_pool")
                hg_in = [sem(f"hg_in{j}") for j in range(2)]
                u_in = [sem(f"u_in{j}") for j in range(2)]
                d_in = [sem(f"d_in{j}") for j in range(2)]
                y_out = [sem(f"ey_out{j}") for j in range(2)]
                names = ("idx_ready", "g_turned", "g_hi", "g_lo", "u_hi", "u_lo", "d_hi", "d_lo", "up_done", "sg_ready", "gated", "a_ready",
                         "a_turned", "a_hi", "a_lo", "down_done", "y_act", "y_dve")
                (idx_ready, g_turned, g_hi, g_lo, u_hi, u_lo, d_hi, d_lo, up_done, sg_ready, gated, a_ready,
                 a_turned, a_hi, a_lo, down_done, y_act, y_dve) = [sem("e_" + n) for n in names]
                block = ctx.enter_context(nc.Block())
                LOOPS = SLOT_TILES // 2
                w1v = w1[0].rearrange("e (k p) n -> p e k n", p=P)
                w3v = w3[0].rearrange("e (k p) n -> p e k n", p=P)
                w2v = w2[0].rearrange("e (k p) n -> p e k n", p=P)

                @block.sync
                def _(sp):
                    sp.dma_start(tok[:], slot_d.rearrange("(p j) a -> p (j a)", p=P)).then_inc(tok_in, 16)
                    with sp.Fori(0, LOOPS) as i:
                        for j in range(2):
                            e = sp.value_load(tile_expert[0:1, bass.ds(i * 2 + j, 1)], min_val=0, max_val=NE - 1)
                            sp.wait_ge(u_lo, i * 2 + j if j else i * 2)
                            sp.dma_start(ur[j][:, :, 0:EH], w1v[:, bass.ds(e, 1)].rearrange("p a k n -> p (a k) n")).then_inc(u_in[j], 16)
                            sp.dma_start(ur[j][:, :, EH:2 * EH], w3v[:, bass.ds(e, 1)].rearrange("p a k n -> p (a k) n")).then_inc(u_in[j], 16)
                            sp.wait_ge(d_lo, i * 2 + j if j else i * 2)
                            sp.dma_start(dr[j][:], w2v[:, bass.ds(e, 1)].rearrange("p a k n -> p (a k) n")).then_inc(d_in[j], 16)

                @block.gpsimd
                def _(pool):
                    pool.wait_ge(tok_in, 16)
                    with pool.Fori(0, LOOPS) as i:
                        for j in range(2):
                            pool.wait_ge(g_turned, i * 2)
                            pool.tensor_copy(idx[j][:], tok[:, bass.ds(i * 2 + j, 1)]).then_inc(idx_ready, 1)
                            pool.wait_ge(idx_ready, i * 2 + (j + 1))
                            pool.sem_inc(waited_pool)
                            pool.indirect_dma_start(hg[j][:], None, h2_d, bass.IndirectOffsetOnAxis(ap=idx[j][:], axis=0))\
                                .then_inc(hg_in[j], 16)
                        for j in range(2):
                            pool.wait_ge(y_act, i * 2 + (j + 1))
                            pool.wait_ge(y_dve, i * 2 + (j + 1))
                            pool.dma_start(moe_d.rearrange("(p j) n -> p j n", p=P)[:, bass.ds(i * 2 + j, 1), :].rearrange("p a n -> p (a n)"),
                                           yo[j][:]).then_inc(y_out[j], 16)
                    for j in range(2):
                        pool.wait_ge(y_out[j], 16 * LOOPS)

                def up(j):
                    return G[:, 4 + j, :]

                @block.tensor
                def _(pe):
                    with pe.Fori(0, LOOPS) as i:
                        for j in range(2):
                            pe.wait_ge(hg_in[j], i * 16 + 16)
                            pe.wait_ge(y_act, i * 2)
                            pe.wait_ge(y_dve, i * 2)
                            for k in range(KD):
                                m = pe.transpose(G[:, 2 * j + k // 4, (k % 4) * P:(k % 4 + 1) * P], hg[j][:, k * P:(k + 1) * P], ident[:])
                            m.then_inc(g_turned, 1)
                        for j in range(2):
                            pe.wait_ge(g_lo, i * 2 + (j + 1))
                            pe.wait_ge(u_lo, i * 2 + (j + 1))
                            pe.wait_ge(a_ready, i * 2)
                            for k in range(KD):
                                for n, (a, w) in enumerate(((ghi, uhi), (ghi, ulo), (glo, uhi))):
                                    m = pe.matmul(up(j), a[j][:, k, :], w[j][:, k, :], start=k == 0 and n == 0, stop=k == KD - 1 and n == 2)
                            m.then_inc(up_done, 1)
                        for j in range(2):
                            pe.wait_ge(a_ready, i * 2 + (j + 1))
                            for k in range(2):
                                m = pe.transpose(TB[:, j, k * P:(k + 1) * P], sg[j][:, k * P:(k + 1) * P], ident[:])
                            m.then_inc(a_turned, 1)
                            pe.wait_ge(a_lo, i * 2 + (j + 1))
                            pe.wait_ge(d_lo, i * 2 + (j + 1))
                            for c in range(2):
                                for k in range(2):
                                    for n, (a, w) in enumerate(((ahi, dhi), (ahi, dlo), (alo, dhi))):
                                        m = pe.matmul(G[:, 2 * j + c, :], a[j][:, k, :], w[j][:, k, c * 512:(c + 1) * 512],
                                                      start=k == 0 and n == 0, stop=k == 1 and n == 2)
                            m.then_inc(down_done, 1)

                @block.scalar
                def _(act):
                    with act.Fori(0, LOOPS) as i:
                        for j in range(2):
                            act.wait_ge(u_in[j], i * 32 + 32)
                            act.wait_ge(up_done, i * 2)
                            act.activation(uhi[j][:], ur[j][:], ACT.Copy).then_inc(u_hi, 1)
                            act.wait_ge(g_turned, i * 2 + (j + 1))
                            act.activation(ghi[j][:].rearrange("p (c k) n -> p c (k n)", c=2), G[:, 2 * j:2 * j + 2, :], ACT.Copy).then_inc(g_hi, 1)
                        for j in range(2):
                            act.wait_ge(d_in[j], i * 16 + 16)
                            act.wait_ge(down_done, i * 2)
                            act.activation(dhi[j][:], dr[j][:], ACT.Copy).then_inc(d_hi, 1)
                            act.wait_ge(up_done, i * 2 + (j + 1))
                            act.activation(sg[j][:], up(j)[:, 0:EH], ACT.Sigmoid).then_inc(sg_ready, 1)
                        for j in range(2):
                            act.wait_ge(a_turned, i * 2 + (j + 1))
                            act.activation(ahi[j][:].rearrange("p k n -> p (k n)"), TB[:, j, 0:EH], ACT.Copy).then_inc(a_hi, 1)
                            act.wait_ge(down_done, i * 2 + (j + 1))
                            act.wait_ge(y_out[j], i * 16)
                            act.activation(yo[j][:, 0:512], G[:, 2 * j, :], ACT.Copy).then_inc(y_act, 1)

                @block.vector
                def _(dve):
                    with dve.Fori(0, LOOPS) as i:
                        for j in range(2):
                            dve.wait_ge(u_hi, i * 2 + (j + 1))
                            dve.tensor_tensor(ulo[j][:], ur[j][:], uhi[j][:].bitcast(F32), ALU.subtract).then_inc(u_lo, 1)
                            dve.wait_ge(g_hi, i * 2 + (j + 1))
                            dve.tensor_tensor(glo[j][:].rearrange("p (c k) n -> p c (k n)", c=2), G[:, 2 * j:2 * j + 2, :],
                                              ghi[j][:].bitcast(F32).rearrange("p (c k) n -> p c (k n)", c=2), ALU.subtract).then_inc(g_lo, 1)
                        for j in range(2):
                            dve.wait_ge(d_hi, i * 2 + (j + 1))
                            dve.tensor_tensor(dlo[j][:], dr[j][:], dhi[j][:].bitcast(F32), ALU.subtract).then_inc(d_lo, 1)
                            dve.wait_ge(sg_ready, i * 2 + (j + 1))
                            dve.tensor_tensor(sg[j][:], up(j)[:, 0:EH], sg[j][:], ALU.mult).then_inc(gated, 1)
                            dve.wait_ge(gated, i * 2 + (j + 1))
                            dve.tensor_tensor(sg[j][:], up(j)[:, EH:2 * EH], sg[j][:], ALU.mult).then_inc(a_ready, 1)
                        for j in range(2):
                            dve.wait_ge(a_hi, i * 2 + (j + 1))
                            dve.tensor_tensor(alo[j][:].rearrange("p k n -> p (k n)"), TB[:, j, 0:EH],
                                              ahi[j][:].bitcast(F32).rearrange("p k n -> p (k n)"), ALU.subtract).then_inc(a_lo, 1)
                            dve.wait_ge(down_done, i * 2 + (j + 1))
                            dve.wait_ge(y_out[j], i * 16)
                            dve.tensor_copy(yo[j][:, 512:1024], G[:, 2 * j + 1, :]).then_inc(y_dve, 1)

        def stage_final(slots, weights):
            ctx = ExitStack()
            with ctx:
                sb, sem = holder(ctx, "final")
                y0 = [sb(f"y0{j}", [P, D]) for j in range(2)]
                y1 = [sb(f"y1{j}", [P, D]) for j in range(2)]
                x1 = [sb(f"x1{j}", [P, D]) for j in range(2)]
                wide = sb("wide", [P, KD, P])
                g2 = [sb(f"g2{j}", [P, D]) for j in range(2)]
                gf = sb("gf", [P, D])
                sqd = sb("sqd", [P, D])
                ss = sb("ss", [P, TT])
                y0_in = [sem(f"y0_in{j}") for j in range(2)]
                y1_in = [sem(f"y1_in{j}") for j in range(2)]
                x1_in = [sem(f"x1_in{j}") for j in range(2)]
                o_out = [sem(f"o_out{j}") for j in range(2)]
                gf_in, wide_ready, g_turned, g2_ready, dve_step, x2_ready, ss_ready, o_ready = (
                    sem("gf_in"), sem("wide_ready"), sem("fg_turned"), sem("g2_ready"), sem("fdve_step"), sem("x2_ready"), sem("ss_ready"), sem("o_ready"))
                block = ctx.enter_context(nc.Block())

                @block.sync
                def _(sp):
                    sp.dma_start(gf[:], g_final.rearrange("(a n) -> a n", a=1).to_broadcast([P, D])).then_inc(gf_in, 16)
                    for t in range(TT + 1):
                        if t < TT:
                            if t >= 2:
                                sp.wait_ge(o_out[t % 2], 16 * (t // 2))
                            sp.dma_start(x1[t % 2][:], x1_d[t * P:(t + 1) * P, :]).then_inc(x1_in[t % 2], 16)
                        if t >= 1:
                            u = t - 1
                            sp.wait_ge(o_ready, u + 1)
                            dst = y_prompt[0, u * P:(u + 1) * P, :] if u < TT - 1 else y_sample.rearrange("b i n -> (b i) n")
                            sp.dma_start(dst, x1[u % 2][:]).then_inc(o_out[u % 2], 16)
                    sp.wait_ge(o_out[0], 16 * ((TT + 1) // 2))
                    sp.wait_ge(o_out[1], 16 * (TT // 2))

                @block.gpsimd
                def _(pool):
                    for t in range(TT):
                        if t >= 2:
                            pool.wait_ge(x2_ready, t - 1)
                        for c, (y, s) in enumerate(((y0, y0_in), (y1, y1_in))):
                            pool.indirect_dma_start(y[t % 2][:], None, moe_d, bass.IndirectOffsetOnAxis(ap=slots[:, c * TT + t:c * TT + t + 1], axis=0))\
                                .then_inc(s[t % 2], 16)

                @block.tensor
                def _(pe):
                    for s in range(2):
                        pe.wait_ge(wide_ready, s + 1)
                        for k in range(KD):
                            m = pe.transpose(G[:, 3 * s + k // 4, (k % 4) * P:(k % 4 + 1) * P], wide[:, k, :], ident[:])
                        m.then_inc(g_turned, 1)

                @block.scalar
                def _(act):
                    for t in range(TT):
                        act.wait_ge(x2_ready, t + 1)
                        act.activation(sqd[:], x1[t % 2][:], ACT.Square, accum_out=ss[:, t:t + 1]).then_inc(ss_ready, 1)
                        act.wait_ge(ss_ready, 2 * t + 1)
                        act.activation(ss[:, t:t + 1], ss[:, t:t + 1], ACT.Sqrt, bias=eps[:, 0:1], scale=1.0 / D).then_inc(ss_ready, 1)

                @block.vector
                def _(dve):
                    for s in range(2):
                        if s:
                            dve.wait_ge(g_turned, s)
                        if s == 0:
                            dve.tensor_copy(wide[:], adaT[:, GATE2:GATE2 + KD, 0:1].to_broadcast([P, KD, P])).then_inc(wide_ready, 1)
                        else:
                            dve.tensor_copy(wide[:].rearrange("p k (b i) -> p k b i", i=NQ),
                                            adaT[:, GATE2:GATE2 + KD, 1:9].unsqueeze(3).to_broadcast([P, KD, NB, NQ])).then_inc(wide_ready, 1)
                    for s in range(2):
                        dve.wait_ge(g_turned, s + 1)
                        dve.tensor_copy(g2[s][:].rearrange("p (c n) -> p c n", n=512), G[:, 3 * s:3 * s + 2, :]).then_inc(g2_ready, 1)
                    dve.wait_ge(g2_ready, 2)
                    dve.wait_ge(gf_in, 16)
                    step = Count(dve_step)

                    def total(t):
                        j = t % 2
                        dve.wait_ge(y0_in[j], 16 * (t // 2 + 1))
                        dve.wait_ge(y1_in[j], 16 * (t // 2 + 1))
                        step.then_wait(dve, dve.tensor_scalar(y0[j][:], y0[j][:], weights[:, 0, t:t + 1], None, ALU.mult))
                        step.then_wait(dve, dve.scalar_tensor_tensor(y0[j][:], y1[j][:], weights[:, 1, t:t + 1], y0[j][:], ALU.mult, ALU.add))
                        step.then_wait(dve, dve.tensor_tensor(y0[j][:], y0[j][:], g2[t // (TT - 1)][:], ALU.mult))
                        dve.wait_ge(x1_in[j], 16 * (t // 2 + 1))
                        dve.tensor_tensor(x1[j][:], x1[j][:], y0[j][:], ALU.add).then_inc(x2_ready, 1)

                    def norm(t):
                        dve.wait_ge(ss_ready, 2 * t + 2)
                        step.then_wait(dve, dve.reciprocal(ss[:, t:t + 1], ss[:, t:t + 1]))
                        dve.scalar_tensor_tensor(x1[t % 2][:], x1[t % 2][:], ss[:, t:t + 1], gf[:], ALU.mult, ALU.mult).then_inc(o_ready, 1)

                    for t in range(TT + 1):
                        if t < TT:
                            total(t)
                        if t >= 1:
                            norm(t - 1)

        mixers = ExitStack()
        with mixers:
            hhi = mixers.enter_context(nc.sbuf_tensor("hhi", [P, KD, T], F32R))
            hlo = mixers.enter_context(nc.sbuf_tensor("hlo", [P, KD, T], F32R))
            with nc.sbuf_tensor("xT", [P, KD, T], F32) as xT:
                stage_start(xT)
                stage_norm(xT, SCALE1, SHIFT1, hhi, hlo)
            stage_forget(hhi, hlo)
            stage_attend(False, hhi, hlo)
            stage_attend(True, hhi, hlo)
            with nc.sbuf_tensor("yhi", [P, KD, T], F32R) as yhi, nc.sbuf_tensor("ylo", [P, KD, T], F32R) as ylo:
                stage_turn_y(yhi, ylo)
                stage_merge(hhi, hlo, yhi, ylo)
        slots = sb("slots", [P, 2 * TT], I32)
        weights = sb("weights", [P, 2, TT])
        tile_expert = sb("tile_expert", [P, SLOT_TILES], I32)
        with nc.sbuf_tensor("xT1", [P, KD, T], F32) as xT:
            stage_out(xT)
            with nc.sbuf_tensor("h2T", [P, KD, T], F32) as h2T:
                stage_norm(xT, SCALE2, SHIFT2, h2T, None)
                stage_route(xT, h2T, slots, weights, tile_expert)
        stage_experts(tile_expert)
        stage_final(slots, weights)


_INS = ['x_prompt', 'x_sample', 'cache_sb_k', 'cache_sb_v', 'cache_fox_k', 'cache_fox_v', 'cache_fox_logf', 'c_prompt', 'c_sample',
        'w_ada', 'b_ada', 'g_mix', 'w_in', 'b_f', 'w_ba', 'w_bb', 'w_gate', 'b_gate', 'w_out', 'g_moe', 'w_rg', 'b_rg', 'w_re', 'b_re',
        'w1', 'w3', 'w2', 'g_final']
_OUTS = [(1, 1024, 1024), (8, 16, 1024)] + [(1, 1, 8, 1024, 64)] * 4 + [(1, 1, 8, 1024)] + [(1, 8, 8, 16, 64)] * 4 + [(1, 8, 8, 16)]


def kernel(**inputs):
    import numpy as _np
    import concourse.bacc as _bacc
    from concourse import mybir as _mybir
    from concourse.bass_utils import run_bass_kernel_spmd as _run

    nc = _bacc.Bacc("TRN2", target_bir_lowering=False, num_devices=1)
    arrays, args = {}, []
    for name in _INS:
        a = _np.ascontiguousarray(inputs[name])
        arrays[f"in_{name}_dram"] = a
        args.append(nc.dram_tensor(f"in_{name}_dram", a.shape, _mybir.dt.from_np(a.dtype), kind="ExternalInput").ap())
    for i, shape in enumerate(_OUTS):
        args.append(nc.dram_tensor(f"out_{i}_dram", shape, _mybir.dt.float32, kind="ExternalOutput").ap())
    program(nc, *args)
    r = _run(nc, [arrays], core_ids=[0])
    return tuple(r.results[0][f"out_{i}_dram"] for i in range(len(_OUTS)))
```
